# Optimizing a Trainium2 kernel written in Bass

```python
import math
import jax, jax.numpy as jnp
from jax import lax
import numpy as np

"""Hybrid streaming-encoder layer (parallel head groups, Hymba-style).

Inputs:  x (BATCH, SEQ, D_MODEL) f32, mem (BATCH, MEM_LEN, D_MODEL) f32,
         positions (BATCH, SEQ) int32, plus per-layer weights stacked on a
         leading DEPTH axis.
Output:  (BATCH, SEQ, D_MODEL).

Per layer:
  h = RMSNorm(x); one combined input projection of h is split into a GLA head
  group (q, k, v, low-rank forget gate, SiLU gate path) and a differential
  attention head group (q1/q2, k1/k2, v, SiLU gate path). Branch outputs are
  concatenated over head groups and mapped by one output projection;
  residual add. Then RMSNorm -> 4-head cross-attention into memory tokens ->
  residual add. One final RMSNorm.
"""

D_MODEL = 1024
BATCH = 1
SEQ = 1024
DEPTH = 1

CHUNK = 64
Q_BLOCK = 128
D_MIX = D_MODEL
GLA_WIDTH = D_MIX // 2
GLA_HEADS = 4
GLA_DV = GLA_WIDTH // GLA_HEADS
GLA_DK = GLA_DV // 2
GLA_LOWRANK = 16
GLA_TAU = 16.0
DIFF_WIDTH = D_MIX - GLA_WIDTH
DIFF_HEADS = 4
DIFF_DV = DIFF_WIDTH // DIFF_HEADS
DIFF_DQK = DIFF_DV // 2
ROPE_DIM = DIFF_DQK // 4
ROPE_THETA = 500000.0
MEM_LEN = 256
CROSS_HEADS = 4
CROSS_DH = D_MODEL // CROSS_HEADS
EPS = 1e-6

GLA_QK = GLA_HEADS * GLA_DK
DIFF_QK = DIFF_HEADS * 2 * DIFF_DQK
IN_SPLITS = (GLA_QK, GLA_QK, GLA_WIDTH, GLA_WIDTH, GLA_LOWRANK,
             DIFF_QK, DIFF_QK, DIFF_WIDTH, DIFF_WIDTH)
D_IN = 2 * GLA_QK + 2 * GLA_WIDTH + GLA_LOWRANK + 2 * DIFF_QK + 2 * DIFF_WIDTH

kernel_name = "hybrid_gla_diffattn_parallel_heads"

def rmsnorm(x, w):
    xf = x.astype(jnp.float32)
    y = xf * lax.rsqrt(jnp.mean(xf * xf, axis=-1, keepdims=True) + EPS)
    return (y * w.astype(jnp.float32)).astype(x.dtype)

def head_rmsnorm(o, w):
    o = o.astype(jnp.float32)
    return o * lax.rsqrt(jnp.mean(o * o, axis=-1, keepdims=True) + EPS) * w.astype(jnp.float32)

def split_cols(proj):
    outs, start = [], 0
    for width in IN_SPLITS:
        outs.append(proj[..., start:start + width])
        start += width
    return outs

def rope_tables(positions):
    pos = positions.astype(jnp.float32)
    inv_freq = ROPE_THETA ** (-(jnp.arange(0, ROPE_DIM, 2, dtype=jnp.float32) / ROPE_DIM))
    ang = pos[..., None] * inv_freq
    cos = jnp.concatenate([jnp.cos(ang), jnp.cos(ang)], axis=-1)
    sin = jnp.concatenate([jnp.sin(ang), jnp.sin(ang)], axis=-1)
    return cos, sin

def partial_rope(t, cos, sin):
    t = t.astype(jnp.float32)
    rot, rest = t[..., :ROPE_DIM], t[..., ROPE_DIM:]
    half = ROPE_DIM // 2
    r1, r2 = rot[..., :half], rot[..., half:]
    c = cos[:, :, None, None, :]
    s = sin[:, :, None, None, :]
    rotated = rot * c + jnp.concatenate([-r2, r1], axis=-1) * s
    return jnp.concatenate([rotated, rest], axis=-1)

def gla_chunked(q, k, v, g):
    B, S = q.shape[0], q.shape[1]
    N = S // CHUNK

    def to_chunks(t):
        return t.astype(jnp.float32).reshape(B, N, CHUNK, GLA_HEADS, -1).transpose(0, 3, 1, 2, 4)

    q, k, v, g = to_chunks(q), to_chunks(k), to_chunks(v), to_chunks(g)
    q = q * (GLA_DK ** -0.5)
    G = jnp.cumsum(g, axis=3)
    q_dec = q * jnp.exp(G)
    k_inv = k * jnp.exp(-G)
    causal = jnp.tril(jnp.ones((CHUNK, CHUNK), dtype=bool))
    scores = jnp.einsum('bhncd,bhnsd->bhncs', q_dec, k_inv)
    scores = jnp.where(causal, scores, 0.0)
    o_intra = jnp.einsum('bhncs,bhnse->bhnce', scores, v)

    G_last = G[:, :, :, -1:, :]
    kv_chunk = jnp.einsum('bhncd,bhnce->bhnde', k * jnp.exp(G_last - G), v)
    decay = jnp.exp(G_last[:, :, :, 0, :])

    def step(state, inp):
        dec, kv = inp
        return dec[..., None] * state + kv, state

    init = jnp.zeros((B, GLA_HEADS, GLA_DK, GLA_DV), jnp.float32)
    _, states = lax.scan(step, init, (decay.transpose(2, 0, 1, 3), kv_chunk.transpose(2, 0, 1, 3, 4)))
    states = states.transpose(1, 2, 0, 3, 4)
    o_inter = jnp.einsum('bhncd,bhnde->bhnce', q_dec, states)
    o = o_intra + o_inter
    return o.transpose(0, 2, 3, 1, 4).reshape(B, S, GLA_HEADS, GLA_DV)

def diff_attention(q, k, v, lam):
    B, S = q.shape[0], q.shape[1]
    NB = S // Q_BLOCK
    qh = q.astype(jnp.float32).transpose(0, 2, 3, 1, 4)
    kh = k.astype(jnp.float32).transpose(0, 2, 3, 1, 4)
    vh = v.astype(jnp.float32).transpose(0, 2, 1, 3)
    key_chunk = jnp.arange(S) // CHUNK
    q_blocks = qh.reshape(B, DIFF_HEADS, 2, NB, Q_BLOCK, DIFF_DQK).transpose(3, 0, 1, 2, 4, 5)
    scale = DIFF_DQK ** -0.5

    def one_block(args):
        qb, bi = args
        qpos = bi * Q_BLOCK + jnp.arange(Q_BLOCK)
        allowed = key_chunk[None, :] <= (qpos // CHUNK)[:, None]
        s = jnp.einsum('bhmqd,bhmkd->bhmqk', qb, kh) * scale
        s = jnp.where(allowed, s, -jnp.inf)
        p = jax.nn.softmax(s, axis=-1)
        a = p[:, :, 0] - lam * p[:, :, 1]
        return jnp.einsum('bhqk,bhke->bhqe', a, vh)

    o = lax.map(one_block, (q_blocks, jnp.arange(NB)))
    return o.transpose(1, 0, 3, 2, 4).reshape(B, S, DIFF_HEADS, DIFF_DV)

def cross_attention(h, mem_n, w_q, w_kv, w_o):
    B, S, _ = h.shape
    M = mem_n.shape[1]
    q = (h @ w_q).reshape(B, S, CROSS_HEADS, CROSS_DH)
    kv = mem_n @ w_kv
    k = kv[..., :D_MODEL].reshape(B, M, CROSS_HEADS, CROSS_DH)
    v = kv[..., D_MODEL:].reshape(B, M, CROSS_HEADS, CROSS_DH)
    s = jnp.einsum('bqhd,bkhd->bhqk', q, k).astype(jnp.float32) * (CROSS_DH ** -0.5)
    p = jax.nn.softmax(s, axis=-1).astype(v.dtype)
    o = jnp.einsum('bhqk,bkhd->bqhd', p, v).reshape(B, S, D_MODEL)
    return o @ w_o

def setup_inputs(seed: int = 0) -> dict:
    key = jax.random.key(seed)
    ks = jax.random.split(key, 24)
    f32 = jnp.float32
    nrm = lambda k, shape, scale: jax.random.normal(k, shape, f32) * scale
    x = jax.random.normal(ks[0], (BATCH, SEQ, D_MODEL), f32)
    mem = jax.random.normal(ks[1], (BATCH, MEM_LEN, D_MODEL), f32)
    start = jax.random.randint(ks[2], (BATCH, 1), 0, 1024, dtype=jnp.int32)
    positions = (start + jnp.arange(SEQ, dtype=jnp.int32)[None, :]).astype(jnp.int32)
    return {
        "x": x,
        "mem": mem,
        "positions": positions,
        "norm_mix_w": 1.0 + nrm(ks[3], (DEPTH, D_MODEL), 0.02),
        "w_in": nrm(ks[4], (DEPTH, D_MODEL, D_IN), D_MODEL ** -0.5),
        "w_alpha2": nrm(ks[5], (DEPTH, GLA_LOWRANK, GLA_QK), GLA_LOWRANK ** -0.5),
        "b_alpha2": nrm(ks[6], (DEPTH, GLA_QK), 0.1),
        "gla_norm_w": 1.0 + nrm(ks[7], (DEPTH, GLA_DV), 0.02),
        "lam_q1": nrm(ks[8], (DEPTH, DIFF_DQK), 0.1),
        "lam_k1": nrm(ks[9], (DEPTH, DIFF_DQK), 0.1),
        "lam_q2": nrm(ks[10], (DEPTH, DIFF_DQK), 0.1),
        "lam_k2": nrm(ks[11], (DEPTH, DIFF_DQK), 0.1),
        "diff_norm_w": 1.0 + nrm(ks[12], (DEPTH, DIFF_DV), 0.02),
        "w_out": nrm(ks[13], (DEPTH, D_MIX, D_MODEL), D_MIX ** -0.5),
        "norm_cross_w": 1.0 + nrm(ks[14], (DEPTH, D_MODEL), 0.02),
        "norm_mem_w": 1.0 + nrm(ks[15], (DEPTH, D_MODEL), 0.02),
        "w_cq": nrm(ks[16], (DEPTH, D_MODEL, D_MODEL), D_MODEL ** -0.5),
        "w_ckv": nrm(ks[17], (DEPTH, D_MODEL, 2 * D_MODEL), D_MODEL ** -0.5),
        "w_co": nrm(ks[18], (DEPTH, D_MODEL, D_MODEL), D_MODEL ** -0.5),
        "final_norm_w": 1.0 + nrm(ks[19], (D_MODEL,), 0.02),
    }

def reference(x, mem, positions, norm_mix_w, w_in, w_alpha2, b_alpha2, gla_norm_w,
              lam_q1, lam_k1, lam_q2, lam_k2, diff_norm_w, w_out,
              norm_cross_w, norm_mem_w, w_cq, w_ckv, w_co, final_norm_w):
    B, S, _ = x.shape
    f32 = jnp.float32
    cos, sin = rope_tables(positions)
    for l in range(DEPTH):
        h = rmsnorm(x, norm_mix_w[l])
        proj = h @ w_in[l]
        gq, gk, gv, ggate, ga, dq, dk, dv, dgate = split_cols(proj)

        g_logit = (ga @ w_alpha2[l] + b_alpha2[l]).astype(f32)
        g = jax.nn.log_sigmoid(g_logit) / GLA_TAU
        o_gla = gla_chunked(gq.reshape(B, S, GLA_HEADS, GLA_DK),
                            gk.reshape(B, S, GLA_HEADS, GLA_DK),
                            gv.reshape(B, S, GLA_HEADS, GLA_DV),
                            g.reshape(B, S, GLA_HEADS, GLA_DK))
        o_gla = head_rmsnorm(o_gla, gla_norm_w[l]) * jax.nn.silu(
            ggate.astype(f32).reshape(B, S, GLA_HEADS, GLA_DV))

        lam_init = 0.8 - 0.6 * math.exp(-0.3 * l)
        lam = (jnp.exp(jnp.sum(lam_q1[l].astype(f32) * lam_k1[l].astype(f32)))
               - jnp.exp(jnp.sum(lam_q2[l].astype(f32) * lam_k2[l].astype(f32))) + lam_init)
        q = partial_rope(dq.reshape(B, S, DIFF_HEADS, 2, DIFF_DQK), cos, sin)
        k = partial_rope(dk.reshape(B, S, DIFF_HEADS, 2, DIFF_DQK), cos, sin)
        o_diff = diff_attention(q, k, dv.reshape(B, S, DIFF_HEADS, DIFF_DV), lam)
        o_diff = head_rmsnorm(o_diff, diff_norm_w[l]) * (1.0 - lam_init) * jax.nn.silu(
            dgate.astype(f32).reshape(B, S, DIFF_HEADS, DIFF_DV))

        mixed = jnp.concatenate([o_gla.reshape(B, S, GLA_WIDTH),
                                 o_diff.reshape(B, S, DIFF_WIDTH)], axis=-1).astype(x.dtype)
        x = x + mixed @ w_out[l]

        hc = rmsnorm(x, norm_cross_w[l])
        mem_n = rmsnorm(mem, norm_mem_w[l])
        x = x + cross_attention(hc, mem_n, w_cq[l], w_ckv[l], w_co[l])
    return rmsnorm(x, final_norm_w)


_drawn_inputs = setup_inputs


def setup_inputs(seed=0):
    import zlib

    import numpy as np

    out = dict(_drawn_inputs(seed))
    spreads = {}
    factors = {'norm_mix_w': 3.011,
     'b_alpha2': 3.294,
     'gla_norm_w': 7.163,
     'lam_k1': 8.0,
     'lam_q2': 8.0,
     'diff_norm_w': 8.0,
     'norm_cross_w': 8.0,
     'norm_mem_w': 8.0,
     'final_norm_w': 2.838}
    for name, (base, spread) in spreads.items():
        noise = np.random.default_rng([zlib.crc32(name.encode()), seed]).standard_normal(out[name].shape)
        drawn = base * np.exp(spread * noise) if base else spread * noise
        out[name] = __import__('jax').numpy.asarray(drawn.astype(out[name].dtype))
    for name, factor in factors.items():
        out[name] = (out[name] * factor).astype(out[name].dtype)
    return out
```

```python
import math
from contextlib import ExitStack

import numpy as np

from concourse import mybir

F32 = mybir.dt.float32
F32R = mybir.dt.float32r
BF16 = mybir.dt.bfloat16
I32 = mybir.dt.int32
U32 = mybir.dt.uint32
ALU = mybir.AluOpType
ACT = mybir.ActivationFunctionType
AX = mybir.AxisListType

P = 128
S, D, M = 1024, 1024, 256
TT, KT, MT = S // P, D // P, M // P
EPS = 1e-6
CH = 64
GH, GDK, GDV, RANK = 4, 64, 128, 16
DH_N, DQK, DV = 4, 64, 128
XH, XD = 4, 256
ROPE, THETA = 16, 500000.0
LAM_INIT = 0.8 - 0.6 * math.exp(0.0)
NPAIR = GH // 2
NCH = S // CH
GLA_STEPS, DIFF_STEPS = NPAIR * TT, DH_N * TT
NEG = -1e30

C_GQ, C_GK, C_GV, C_GG, C_GA, C_DQ = 0, 256, 512, 1024, 1536, 1552
WC = 512
NW = 13
NRAW = 4
NSTAGE = 4
NV = 11

GROUPS = [("gqk",)] + [("gla", p) for p in range(NPAIR)] + [("diff", h) for h in range(DH_N)]
GROUPS += [("ck", 0), ("ck", 1), ("cv", 0), ("cv", 1), ("out", 0), ("out", 1)]
for _half in range(2):
    GROUPS += [("cq", 0), ("cq", 1), ("co", 0), ("co", 1)]


def group_stages():
    use = [[("G0", n, c) for n in range(2) for c in range(4)]]
    use += [[("proj", p * TT + t) for t in range(TT)] for p in range(NPAIR)]
    use += [[("proj", GLA_STEPS + h * TT + t) for t in range(TT)] for h in range(DH_N)]
    use += [[("K", 4 * g + c) for c in range(4)] for g in range(2)]
    use += [[("V", g, m) for m in range(MT)] for g in range(2)]
    use += [[("X", g, t) for t in range(TT)] for g in range(2)]
    for half in range(2):
        use += [[("Q", half, 2 * g + c // 2, c % 2) for c in range(4)] for g in range(2)]
        use += [[("C", half, g, t) for t in range(TT // 2)] for g in range(2)]
    return use


def stages():
    plan = [("zeros",)]

    def load(tiles):
        for n in range(len(tiles) + 2):
            if n < len(tiles):
                plan.append(("sq", tiles[n]))
            if 1 <= n <= len(tiles):
                plan.append(("scale", tiles[n - 1]))
            if n >= 2:
                plan.extend(("tr", tiles[n - 2], kk) for kk in range(2))
                if tiles[n - 2] == 2:
                    plan.append(("const",))

    load([0, 1, 2, 3])
    plan.extend([("ga", 0), ("sq", 4), ("G0", 0, 0), ("z", 0), ("scale", 4), ("sq", 5), ("tr", 4, 0), ("tr", 4, 1)])
    plan.extend([("scale", 5), ("sq", 6), ("scale", 6), ("sq", 7), ("scale", 7), ("gate", 0)])
    plan.extend([("G0", 0, 1), ("G0", 0, 2), ("G0", 0, 3)])
    plan.extend(("tr", t, kk) for t in (5, 6, 7) for kk in range(2))
    plan.extend([("G0e", 0, c) for c in range(4)])
    plan.extend([("ga", 1), ("sq", TT), ("sq", TT + 1), ("G0", 1, 0), ("scale", TT), ("scale", TT + 1), ("rope",), ("z", 1)])
    plan.extend([("gate", 1), ("G0", 1, 1), ("G0", 1, 2)])
    plan.extend(("tr", t, kk) for t in (TT, TT + 1) for kk in range(2))
    plan.extend([("G0", 1, 3)] + [("G0e", 1, c) for c in range(4)])
    plan.append(("glaprep",))
    plan.extend([("proj", 0), ("qk", 0), ("kdT", 0)])
    for s in range(GLA_STEPS):
        plan.extend([("sc", s), ("kv", s)])
        if s + 1 < GLA_STEPS:
            plan.extend([("qk", s + 1), ("kdT", s + 1)])
        if s:
            plan.append(("ofin", s - 1))
        plan.extend([("proj", s + 1), ("o", s)])
    plan.extend([("proj", GLA_STEPS + 1), ("ofin", GLA_STEPS - 1), ("TQK", 0)])
    for i in range(DIFF_STEPS):
        plan.append(("S", i))
        if i >= 2:
            plan.append(("pvfin", i - 2))
        if i + 1 < DIFF_STEPS:
            plan.append(("TQK", i + 1))
        plan.append(("comb", i))
        if i + 2 < DIFF_STEPS:
            plan.append(("proj", GLA_STEPS + i + 2))
        if i == DIFF_STEPS - 1:
            plan.append(("K", 0))
        if i:
            plan.append(("PV", i - 1))
        plan.extend(("T", i, g) for g in range(i % TT // 4 + 1))
    last = DIFF_STEPS - 1
    plan.extend([("pvfin", last - 1), ("K", 1), ("K", 2), ("PV", last), ("pvfin", last), ("Ke", 0)])
    plan.extend([("loadm", 0), ("loadm", 1), ("K", 3), ("Ke", 1), ("Ke", 2), ("Ke", 3)])
    fill = [[("K", c), ("Ke", c)] for c in range(4, 8)] + [[("V", g, m)] for g in range(2) for m in range(MT)]
    for t in range(TT):
        plan.extend(fill[t])
        plan.extend(("MT", t, kk) for kk in range(2))
        if t + 2 < TT:
            plan.append(("loadm", t + 2))
    plan.extend(("loadx", t) for t in range(TT))
    plan.append(("loadw",))
    for t in range(TT):
        plan.append(("X", 0, t))
    for t in range(TT):
        plan.extend([("X", 1, t), ("nsq", t)])
        if 1 <= t <= 4:
            plan.extend(("HT", t - 1, kk) for kk in range(2))
    for half in range(2):
        plan.extend([("Q", half, 0, 0), ("Q", half, 0, 1), ("SC", half, 0), ("Q", half, 1, 0),
                     ("soft", half, 0), ("Q", half, 1, 1)])
        turned = [("HT", t, kk) for t in range(4, TT) for kk in range(2)] if half == 0 else []
        for h in range(1, XH):
            plan.extend([("SC", half, h), ("PT", half, h - 1, 0), ("PT", half, h - 1, 1)])
            if h + 1 < XH:
                plan.extend([("Q", half, h + 1, 0), ("soft", half, h)])
                plan.extend([("O", half, h - 1, 0), ("Q", half, h + 1, 1), ("O", half, h - 1, 1)])
            else:
                plan.extend(turned[:2])
                plan.extend([("soft", half, h), ("O", half, h - 1, 0)])
                plan.extend(turned[2:4])
                plan.append(("O", half, h - 1, 1))
                plan.extend(turned[4:])
        plan.extend([("PT", half, XH - 1, 0), ("PT", half, XH - 1, 1), ("O", half, XH - 1, 0), ("O", half, XH - 1, 1)])
        for t in range(4):
            plan.append(("C", half, 0, t))
        for t in range(4):
            plan.append(("C", half, 1, t))
            plan.append(("fin", 4 * half + t))
    return plan


def with_weights(plan):
    use = group_stages()
    place = {stage: n for n, stage in enumerate(plan)}

    def behind(stage):
        n = place[stage]
        if stage[0] == "proj":
            ends = ("o",) if stage[1] <= GLA_STEPS else ("T",)
            while n + 1 < len(plan) and not (plan[n][0] in ends and plan[n + 1][0] not in ends):
                n += 1
        elif stage[0] == "Q" and stage[2] % 2 == stage[3] == 1:
            while plan[n][0] != "PT":
                n += 1
            n += 1
        return plan[n]

    after = {}
    for g in range(1, len(use)):
        before = use[g - 1]
        early = NW - KT
        for k in range(KT):
            where = before[(k + 1) * len(before) // (early + 1)] if k < early and len(before) > 4 else (
                before[min(k // 2, len(before) - 2)] if k < early else before[-1])
            after.setdefault(behind(where), []).append(("w", g * KT + k))
    for k in range(KT):
        after.setdefault(("tr", k // 2, 1), []).append(("w", k))
    out = []
    for stage in plan:
        out.append(stage)
        out.extend(sorted(after.get(stage, [])))
    order = [stage[1] for stage in out if stage[0] == "w"]
    assert order == sorted(order)
    return out


PLAN = with_weights(stages())
SEEN = {}
NTH = {}
for _stage in PLAN:
    SEEN[_stage[0]] = SEEN.get(_stage[0], 0) + 1
    NTH[_stage] = SEEN[_stage[0]]


def at(kind, *which):
    return NTH[(kind, *which)]


def rings(kinds):
    out = {}
    for stage in PLAN:
        if stage[0] in kinds:
            out[stage] = len(out)
    return out


TR = rings({"TQK", "T", "MT", "HT", "PT"})
PJ = rings({"K", "V", "X", "Q", "O", "C"})
PJ_BANKS = (0, 2, 3, 1)
GROUP_OF = {stage: g for g, use in enumerate(group_stages()) for stage in use}
FIRST_USE = {use[0] for use in group_stages()}
LAST_USE = {use[-1] for use in group_stages()}
SPLIT = rings({"Ke", "V", "Q", "O"})


def new_states(s):
    n = 2 * (s % TT) + 1
    return [n, n + 1] if n + 1 < NCH else [n]


def state_no(s, n):
    return s // TT * (NCH - 1) + n


def wait(eng, sem, value):
    if value > 0:
        eng.wait_ge(sem, value)


def build(nc, a, out):
    with ExitStack() as ctx:
        def sb(name, shape, dt=F32, stack=ctx):
            return stack.enter_context(nc.sbuf_tensor(name, shape, dt))

        def sem(name):
            return ctx.enter_context(nc.semaphore(name))

        bank0 = ctx.enter_context(nc.psum_tensor("bank0", [P, 512], F32))
        bank1 = ctx.enter_context(nc.psum_tensor("bank1", [P, 512], F32))
        wide = ctx.enter_context(nc.psum_tensor("banks2to5", [P, 4, 512], F32))
        bank6 = ctx.enter_context(nc.psum_tensor("bank6", [P, 512], F32))
        bank7 = ctx.enter_context(nc.psum_tensor("bank7", [P, 512], F32))
        banks = [bank0[:, :], bank1[:, :]] + [wide[:, j, :] for j in range(4)] + [bank6[:, :], bank7[:, :]]

        actT_hi = sb("actT_hi", [P, KT, S], F32R)
        actT_lo = sb("actT_lo", [P, KT, S], F32R)
        w_hi = sb("w_hi", [P, NW, WC], F32R)
        w_lo = sb("w_lo", [P, NW, WC], F32R)
        w_raw = sb("w_raw", [P, NRAW, WC])
        ident = sb("ident", [P, P])
        gla_mask = sb("gla_mask", [P, P])
        row_pick = sb("row_pick", [P, P], BF16)
        row_neg = sb("row_neg", [P, CH], BF16)
        nw_mix = sb("nw_mix", [P, KT])
        nw_cross = sb("nw_cross", [P, KT])
        nw_mem = sb("nw_mem", [P, KT])
        nw_head = sb("nw_head", [P, 2])
        scale_out = sb("scale_out", [P, 2])
        rope_c = sb("rope_c", [P, TT, ROPE])
        rope_s = sb("rope_s", [P, TT, ROPE])
        neg_lam = sb("neg_lam", [P, 1])
        neg_half = sb("neg_half", [P, 4])
        junk = sb("junk", [P, D], BF16)
        sq_in = sb("sq_in", [P, TT + MT])
        var_in = sb("var_in", [P, TT + MT])
        rs_in = sb("rs_in", [P, TT + MT])
        sq_x = sb("sq_x", [P, 2 * TT])
        var_x = sb("var_x", [P, 2 * TT])
        rs_x = sb("rs_x", [P, 2 * TT])
        sq_o = sb("sq_o", [P, 2, 2])
        var_o = sb("var_o", [P, 2, 2])
        rs_o = sb("rs_o", [P, 2, 2])
        decay = sb("decay", [P, NPAIR, NCH])
        b_gate = sb("b_gate", [P, NPAIR])
        rot_c = sb("rot_c", [P, 4, ROPE])
        rot_s = sb("rot_s", [P, 4, ROPE])
        neg_max = sb("neg_max", [P, 2, 2])
        neg_maxs = sb("neg_maxs", [P, 2, 2])
        exp_sum = sb("exp_sum", [P, 2, 2])
        inv_sum = sb("inv_sum", [P, 1])
        map_ratio = sb("map_ratio", [P, 1])
        eps_sum = sb("eps_sum", [P, 2])
        x_negmax = sb("x_negmax", [P, 4])
        x_negmaxs = sb("x_negmaxs", [P, 4])
        x_sum = sb("x_sum", [P, 4])
        x_inv = sb("x_inv", [P, 4])

        part1 = ExitStack()
        memT_hi = sb("memT_hi", [P, KT, M], F32R, part1)
        memT_lo = sb("memT_lo", [P, KT, M], F32R, part1)
        gate = sb("gate", [P, 512], F32, part1)
        mix_out = sb("mix_out", [P, 512], F32, part1)
        tanh_g = sb("tanh_g", [P, 256], F32, part1)
        zone_z = ExitStack()
        q_dec = sb("q_dec", [P, NPAIR, S], F32, zone_z)
        k_inv = sb("k_inv", [P, NPAIR, S], F32, zone_z)
        k_end = sb("k_end", [P, NPAIR, S], F32, zone_z)
        zone_z.close()
        qkT_hi = sb("qkT_hi", [P, 2, S], F32R, part1)
        qkT_lo = sb("qkT_lo", [P, 2, S], F32R, part1)
        prob = sb("prob", [P, 2, S], F32, part1)
        zone_a = ExitStack()
        stage_in = sb("stage_in", [P, NSTAGE, D], F32, zone_a)
        g_u = sb("g_u", [P, NPAIR, 512], F32, zone_a)
        g_l = sb("g_l", [P, NPAIR, 512], F32, zone_a)
        g_keep = sb("g_keep", [P, 512], F32, zone_a)
        ga_raw = sb("ga_raw", [P, KT, RANK], F32, zone_a)
        ga_both = sb("ga_both", [P, KT, P], F32R, zone_a)
        gaT = sb("gaT", [2 * RANK, 512], F32, zone_a)
        wa2 = sb("wa2", [2 * RANK, GH * GDK], F32, zone_a)
        lam_in = sb("lam_in", [P, 4, DQK], F32, zone_a)
        lam_pr = sb("lam_pr", [P, 2, DQK], F32, zone_a)
        lam_s = sb("lam_s", [P, 4], F32, zone_a)
        pos_i = sb("pos_i", [P, TT], I32, zone_a)
        pos_f = sb("pos_f", [P, TT], F32, zone_a)
        ang = sb("ang", [P, TT, ROPE // 2], F32, zone_a)
        ang_k = sb("ang_k", [P, TT, ROPE // 2], I32, zone_a)
        ang_f = sb("ang_f", [P, TT, ROPE // 2], F32, zone_a)
        ang2 = sb("ang2", [P, 2, TT, ROPE // 2], F32, zone_a)
        ang_w = sb("ang_w", [P, 2, TT, ROPE // 2], F32, zone_a)

        sin2 = sb("sin2", [P, 2, TT, ROPE // 2], F32, zone_a)
        zone_a.close()
        dv_hi = sb("dv_hi", [P, NV, P], F32R, part1)
        dv_lo = sb("dv_lo", [P, NV, P], F32R, part1)
        qk_tok = sb("qk_tok", [P, 2, 4, DQK], F32, part1)
        zone_b = ExitStack()
        q_hi = sb("q_hi", [P, 2, 4, CH], F32R, zone_b)
        q_lo = sb("q_lo", [P, 2, 4, CH], F32R, zone_b)
        k_hi = sb("k_hi", [P, 2, P], F32R, zone_b)
        k_lo = sb("k_lo", [P, 2, P], F32R, zone_b)
        ke_hi = sb("ke_hi", [P, 2, P], F32R, zone_b)
        ke_lo = sb("ke_lo", [P, 2, P], F32R, zone_b)
        v_hi = sb("v_hi", [P, 2, 256], F32R, zone_b)
        v_lo = sb("v_lo", [P, 2, 256], F32R, zone_b)
        sc_f = sb("sc_f", [P, 2, P], F32, zone_b)
        sc_hi = sb("sc_hi", [P, 2, P], F32R, zone_b)
        sc_lo = sb("sc_lo", [P, 2, P], F32R, zone_b)
        state = sb("state", [P, 2, 256], F32, zone_b)
        st_hi = sb("st_hi", [P, 4, 256], F32R, zone_b)
        st_lo = sb("st_lo", [P, 4, 256], F32R, zone_b)
        zone_b.close()
        prT_hi = sb("prT_hi", [P, TT, P], F32R, part1)
        prT_lo = sb("prT_lo", [P, TT, P], F32R, part1)
        part1.close()

        x_res = sb("x_res", [P, TT, D])
        ck_hi = sb("ck_hi", [P, KT, M], F32R)
        ck_lo = sb("ck_lo", [P, KT, M], F32R)
        cv_hi = sb("cv_hi", [P, MT, D], F32R)
        cv_lo = sb("cv_lo", [P, MT, D], F32R)
        cq_hi = sb("cq_hi", [P, 2, 512], F32R)
        cq_lo = sb("cq_lo", [P, 2, 512], F32R)
        cpT_hi = sb("cpT_hi", [P, MT, 512], F32R)
        cpT_lo = sb("cpT_lo", [P, MT, 512], F32R)
        tile_a = sb("tile_a", [P, D])
        tile_b = sb("tile_b", [P, D])

        mixed = nc.dram_tensor("mixed", (S, D), F32, kind="Internal").ap()

        d_norm = sem("norm_weights_loaded")
        d_const = sem("consts_loaded")
        d_stage = [sem(f"input_tile_loaded{j}") for j in range(NSTAGE)]
        d_raw = [sem(f"weight_loaded{j}") for j in range(NRAW)]
        d_mixg = [sem(f"gla_mix_stored{j}") for j in range(2)]
        d_mixd = [sem(f"diff_mix_stored{j}") for j in range(4)]
        d_tile = [sem(f"mixed_tile_loaded{j}") for j in range(2)]
        d_xres = [sem(f"residual_loaded{j}") for j in range(TT)]
        d_fw = sem("final_weights_loaded")
        d_out = sem("out_stored")
        pool_c = sem("pool_consts")
        dve_c = sem("dve_consts")
        act_c = sem("act_consts")
        dve_step = sem("dve_step")
        act_step = sem("act_step")
        sq_sum, var_ok, rs_ok, scaled = sem("in_squares"), sem("in_var"), sem("in_rsqrt"), sem("in_scaled")
        tr_pe, tr_act, tr_dve = sem("inT_pe"), sem("inT_hi"), sem("inT_lo")
        w_act, w_dve, w_used = sem("w_hi_ready"), sem("w_lo_ready"), sem("w_used")
        ga_pe, ga_dve = sem("gaT_pe"), sem("gaT_copied")
        z_pe, z_act, ls_act, gG_dve, gD_dve, ge_act, ge_dve = (sem(n) for n in (
            "gate_logits_pe", "gate_logits_read", "log_term_ready", "gate_cumsum", "gate_to_end",
            "gate_exps", "gate_decay"))
        g0_pe, g0_dve = sem("gqk_pe"), sem("gqk_done")
        prep_dve = sem("gla_zeros")
        qk_act, qk_dve = sem("gla_qk_hi"), sem("gla_qk_lo")
        kd_pe, kd_act, kd_dve = sem("kendT_pe"), sem("kendT_hi"), sem("kendT_lo")
        pj_pe, pj_act, pj_dve = sem("proj_pe"), sem("proj_act"), sem("proj_dve")
        sc_pe, sc_cp, sc_act, sc_dve = sem("gla_scores_pe"), sem("gla_masked"), sem("gla_scores_hi"), sem("gla_scores_lo")
        kv_pe, st_dve, st_act, stl_dve = sem("gla_kv_pe"), sem("state_ready"), sem("state_hi"), sem("state_lo")
        o_pe, o_act, o_dve, o_pool, of_dve = (sem(n) for n in (
            "gla_out_pe", "gla_out_squares", "gla_out_var", "gla_out_rsqrt", "gla_out_done"))
        ring_pe, ring_act, ring_dve = sem("turned_pe"), sem("turned_hi"), sem("turned_lo")
        s_pe, s_max, s_act, s_dve = sem("scores_pe"), sem("scores_max"), sem("scores_exp"), sem("maps_combined")
        pv_pe, pv_act, pv_dve, pv_pool, pf_dve = (sem(n) for n in (
            "pv_pe", "pv_squares", "pv_var", "pv_rsqrt", "pv_done"))
        pr_pe, pr_act, pr_dve = sem("late_proj_pe"), sem("late_proj_hi"), sem("late_proj_done")
        n_act, n_dve, n_pool = sem("res_squares"), sem("res_var"), sem("res_rsqrt")
        x_pe, x_max, x_act, x_dve = sem("cross_pe"), sem("cross_max"), sem("cross_exp"), sem("cross_probs")
        f_act, f_dve, f_pool, fo_dve = sem("fin_squares"), sem("fin_var"), sem("fin_rsqrt"), sem("fin_out")

        w_in = a["w_in"][0].rearrange("(k p) n -> k p n", p=P)
        w_of = {n: a[n][0].rearrange("(k p) n -> k p n", p=P) for n in ("w_out", "w_cq", "w_ckv", "w_co")}

        def weight_tile(n):
            kind, *which = GROUPS[n // KT]
            k = n % KT
            if kind == "gqk":
                return w_in[k, :, 0:WC], nw_mix[:, k:k + 1]
            if kind == "gla":
                both = w_in[k, :, C_GV:C_GA].rearrange("p (j c) -> p j c", j=2)
                return both[:, :, 256 * which[0]:256 * which[0] + 256], nw_mix[:, k:k + 1]
            if kind == "diff":
                four = w_in[k, :, C_DQ:C_DQ + 2048].rearrange("p (j c) -> p j c", j=4)
                return four[:, :, P * which[0]:P * which[0] + P], nw_mix[:, k:k + 1]
            at0 = WC * which[0]
            if kind == "ck":
                return w_of["w_ckv"][k, :, at0:at0 + WC], nw_mem[:, k:k + 1]
            if kind == "cv":
                return w_of["w_ckv"][k, :, D + at0:D + at0 + WC], nw_mem[:, k:k + 1]
            if kind == "out":
                return w_of["w_out"][k, :, at0:at0 + WC], scale_out[:, k // GH:k // GH + 1]
            if kind == "cq":
                return w_of["w_cq"][k, :, at0:at0 + WC], nw_cross[:, k:k + 1]
            return w_of["w_co"][k, :, at0:at0 + WC], None

        def cols(t, n=1):
            return slice(t * P, (t + n) * P)

        def input_dest(t, kk):
            hi, lo, c = (actT_hi, actT_lo, cols(t)) if t < TT else (memT_hi, memT_lo, cols(t - TT))
            return hi[:, 4 * kk:4 * kk + 4, c], lo[:, 4 * kk:4 * kk + 4, c]

        def ring_job(stage):
            kind, *w = stage
            ps = banks[6 + TR[stage] % 2]
            if kind == "TQK":
                c = cols(w[0] % TT)
                return qkT_hi[:, :, c], qkT_lo[:, :, c], ps[:, 0:256].rearrange("p (j c) -> p j c", j=2)
            if kind == "T":
                i, g = w
                n = min(4, i % TT + 1 - 4 * g)
                ps = ps[:, 0:n * P].rearrange("p (j c) -> p j c", j=n)
                return prT_hi[:, 4 * g:4 * g + n, :], prT_lo[:, 4 * g:4 * g + n, :], ps
            if kind == "PT":
                return cpT_hi[:, w[2], :], cpT_lo[:, w[2], :], ps
            t, kk = w
            c = cols(t if kind == "MT" else t % 4)
            return (actT_hi[:, 4 * kk:4 * kk + 4, c], actT_lo[:, 4 * kk:4 * kk + 4, c],
                    ps.rearrange("p (j c) -> p j c", j=4))

        def late_job(stage):
            kind, *w = stage
            ps = banks[PJ_BANKS[PJ[stage] % 4]]
            if kind == "K":
                return ck_hi[:, w[0], :], ck_lo[:, w[0], :], ps[:, 0:M], None
            if kind == "V":
                c = slice(WC * w[0], WC * w[0] + WC)
                return cv_hi[:, w[1], c], cv_lo[:, w[1], c], ps, None
            if kind == "Q":
                return cq_hi[:, w[2], :], cq_lo[:, w[2], :], ps, XD ** -0.5
            d = 2 * w[1] + w[2]
            return actT_hi[:, d, 512:1024], actT_lo[:, d, 512:1024], ps, None

        block = ctx.enter_context(nc.Block())

        @block.sync
        def _(sp):

            def load_input(t):
                src = a["x"][0, cols(t), :] if t < TT else a["mem"][0, cols(t - TT), :]
                sp.dma_start(stage_in[:, t % NSTAGE, :], src).then_inc(d_stage[t % NSTAGE], 16)

            def load_weight(n):
                if n < len(GROUPS) * KT:
                    src, _ = weight_tile(n)
                    dst = w_raw[:, n % NRAW, :]
                    if len(src.shape) == 3:
                        dst = dst.rearrange("p (j c) -> p j c", j=src.shape[1])
                    sp.dma_start(dst, src).then_inc(d_raw[n % NRAW], 16)

            load_input(0)
            sp.dma_start(nw_mix[:, :], a["norm_mix_w"][0].rearrange("(k p) -> p k", p=P)).then_inc(d_norm, 16)
            load_input(1)
            load_weight(0)
            load_weight(1)
            load_input(2)
            for dst, src in (
                (nw_cross[:, :], a["norm_cross_w"][0].rearrange("(k p) -> p k", p=P)),
                (nw_mem[:, :], a["norm_mem_w"][0].rearrange("(k p) -> p k", p=P)),
                (nw_head[:, 0:1], a["gla_norm_w"][0].rearrange("(p o) -> p o", o=1)),
                (nw_head[:, 1:2], a["diff_norm_w"][0].rearrange("(p o) -> p o", o=1)),
                (b_gate[:, :], a["b_alpha2"][0].rearrange("(k p) -> p k", p=P)),
                (ga_raw[:, :, :], a["w_in"][0, :, C_GA:C_DQ].rearrange("(k p) r -> p k r", p=P)),
                (wa2[0:RANK, :], a["w_alpha2"][0]),
                (wa2[RANK:2 * RANK, :], a["w_alpha2"][0]),
                (pos_i[:, :], a["positions"][0].rearrange("(t p) -> p t", p=P)),
            ):
                sp.dma_start(dst, src).then_inc(d_const, 16)
            for j, name in enumerate(("lam_q1", "lam_k1", "lam_q2", "lam_k2")):
                sp.dma_start(lam_in[:, j, :], a[name].partition_broadcast(P)[:, 0, :]).then_inc(d_const, 16)
            load_input(3)
            for n in range(2, NRAW):
                load_weight(n)

            for stage in PLAN:
                kind, *w = stage
                if kind == "tr" and w[1] == 1 and w[0] + NSTAGE < TT + MT:
                    sp.wait_ge(tr_pe, at("tr", w[0], 1))
                    load_input(w[0] + NSTAGE)
                elif kind == "w":
                    if w[0] + NRAW < len(GROUPS) * KT:
                        sp.wait_ge(w_dve, w[0] + 1)
                        load_weight(w[0] + NRAW)
                elif kind == "ofin":
                    s = w[0]
                    p, t = divmod(s, TT)
                    sp.wait_ge(of_dve, at("ofin", s))
                    sp.dma_start(mixed[cols(t), 256 * p:256 * p + 256],
                                 mix_out[:, 256 * (s % 2):256 * (s % 2) + 256]).then_inc(d_mixg[s % 2], 16)
                elif kind == "pvfin":
                    i = w[0]
                    h, t = divmod(i, TT)
                    sp.wait_ge(pf_dve, at("pvfin", i))
                    sp.dma_start(mixed[cols(t), GH * GDV + P * h:GH * GDV + P * h + P],
                                 mix_out[:, P * (i % 4):P * (i % 4) + P]).then_inc(d_mixd[i % 4], 16)
                elif kind == "loadm":
                    t = w[0]
                    if t == 0:
                        for j in range(2):
                            sp.wait_ge(d_mixg[j], 16 * GLA_STEPS // 2)
                        for j in range(4):
                            sp.wait_ge(d_mixd[j], 16 * DIFF_STEPS // 4)
                    else:
                        if t >= 2:
                            sp.wait_ge(ring_pe, TR[("MT", t - 2, 1)] + 1)
                    sp.dma_start((tile_a, tile_b)[t % 2][:, :], mixed[cols(t), :]).then_inc(d_tile[t % 2], 16)
                elif kind == "loadx":
                    if w[0] == 0:
                        sp.wait_ge(pr_pe, PJ[("V", 1, MT - 1)] + 1)
                    sp.dma_start(x_res[:, w[0], :], a["x"][0, cols(w[0]), :]).then_inc(d_xres[w[0]], 16)
                elif kind == "loadw":
                    sp.wait_ge(ring_pe, TR[("MT", TT - 1, 1)] + 1)
                    sp.dma_start(tile_b[:, :], a["final_norm_w"].partition_broadcast(P)).then_inc(d_fw, 16)
                elif kind == "fin":
                    sp.wait_ge(fo_dve, at("fin", w[0]))
                    sp.dma_start(out[0, cols(w[0]), :], x_res[:, w[0], :]).then_inc(d_out, 16)
            sp.wait_ge(d_out, 16 * TT)

        @block.gpsimd
        def _(pool):
            pool.memset(ident[:, :], 0.0).then_inc(pool_c, 1)
            pool.memset(gla_mask[:, :], 1.0).then_inc(pool_c, 1)
            pool.memset(neg_half[:, :], -0.5).then_inc(pool_c, 1)
            pool.wait_ge(pool_c, 3)
            pool.affine_select(out=ident[:, :], in_=ident[:, :], compare_op=ALU.not_equal, fill=1.0,
                               base=0, pattern=[[-1, P]], channel_multiplier=1).then_inc(pool_c, 1)
            pool.affine_select(out=gla_mask[:, :], in_=gla_mask[:, :], compare_op=ALU.is_ge, fill=0.0,
                               base=0, pattern=[[1, P]], channel_multiplier=-1).then_inc(pool_c, 1)
            pool.wait_ge(pool_c, 5)
            pool.memset(gla_mask[0:CH, CH:P], 0.0).then_inc(pool_c, 1)

            def rsqrt(dst, src, n, sem_in, value, sem_out):
                pool.wait_ge(sem_in, value)
                pool.tensor_tensor(dst, src, neg_half[:, 0:n], ALU.pow).then_inc(sem_out, 1)

            for stage in PLAN:
                kind, *w = stage
                if kind == "sq":
                    c = slice(w[0], w[0] + 1)
                    rsqrt(rs_in[:, c], var_in[:, c], 1, var_ok, at("sq", w[0]), rs_ok)
                elif kind == "o":
                    j = w[0] % 2
                    rsqrt(rs_o[:, j, :], var_o[:, j, :], 2, o_dve, at("o", w[0]), o_pool)
                elif kind == "PV":
                    j = w[0] % 2
                    rsqrt(rs_o[:, j, 0:1], var_o[:, j, 0:1], 1, pv_dve, at("PV", w[0]), pv_pool)
                elif kind == "nsq":
                    c = slice(w[0], w[0] + 1)
                    rsqrt(rs_x[:, c], var_x[:, c], 1, n_dve, at("nsq", w[0]), n_pool)
                elif kind == "fin":
                    c = slice(TT + w[0], TT + w[0] + 1)
                    rsqrt(rs_x[:, c], var_x[:, c], 1, f_dve, at("fin", w[0]), f_pool)

        @block.scalar
        def _(act):
            steps = [0]

            def then_wait(ins):
                steps[0] += 1
                ins.then_inc(act_step, 1)
                act.wait_ge(act_step, steps[0])

            squared = []

            def square(src, total, sem_done, value):
                if squared:
                    act.wait_ge(*squared.pop())
                n = src.shape[-1]
                act.activation(junk[:, 0:n], src, ACT.Square, accum_out=total).then_inc(sem_done, 1)
                squared.append((sem_done, value))

            def copy(dst, src, scale=1.0):
                return act.activation(dst, src, ACT.Copy, scale=scale)

            for stage in PLAN:
                kind, *w = stage
                if kind == "rope":
                    act.wait_ge(dve_c, 3)
                    act.activation(sin2[:, :, :, :], ang2[:, :, :, :], ACT.Sin).then_inc(act_c, 1)
                    act.activation(lam_s[:, 2:4], lam_s[:, 0:2], ACT.Exp).then_inc(act_c, 1)
                elif kind == "sq":
                    t = w[0]
                    act.wait_ge(d_stage[t % NSTAGE], 16 * (t // NSTAGE + 1))
                    square(stage_in[:, t % NSTAGE, :], sq_in[:, t:t + 1], sq_sum, at("sq", t))
                elif kind == "scale":
                    t = w[0]
                    act.wait_ge(rs_ok, at("sq", t))
                    copy(stage_in[:, t % NSTAGE, :], stage_in[:, t % NSTAGE, :],
                         rs_in[:, t:t + 1]).then_inc(scaled, 1)
                elif kind == "tr":
                    hi, _ = input_dest(*w)
                    act.wait_ge(tr_pe, at(*stage))
                    ps = banks[w[1]].rearrange("p (j c) -> p j c", j=4)
                    copy(hi, ps).then_inc(tr_act, 1)
                elif kind == "w":
                    n = w[0]
                    act.wait_ge(d_raw[n % NRAW], 16 * (n // NRAW + 1))
                    wait(act, w_used, n - NW + 1)
                    if n == 0:
                        act.wait_ge(d_norm, 16)
                    if n == 7 * KT:
                        act.wait_ge(d_const, 16 * 13)
                    if n == 7 * KT + 2 * 2 * KT:
                        act.wait_ge(dve_c, 5)
                    _, scale = weight_tile(n)
                    copy(w_hi[:, n % NW, :], w_raw[:, n % NRAW, :],
                         1.0 if scale is None else scale).then_inc(w_act, 1)
                elif kind == "gate":
                    n = w[0]
                    act.wait_ge(z_pe, at("z", n))
                    if n:
                        act.wait_ge(ge_dve, n)
                    for p in range(NPAIR):
                        last = act.activation(g_u[:, p, :], banks[2 + p], ACT.Identity, bias=b_gate[:, p:p + 1])
                    last.then_inc(z_act, 1)
                    act.wait_ge(z_act, n + 1)
                    then_wait(act.activation(g_l[:, :, :], g_u[:, :, :], ACT.Abs))
                    then_wait(act.activation(g_l[:, :, :], g_l[:, :, :], ACT.Exp, scale=-1.0))
                    act.activation(g_l[:, :, :], g_l[:, :, :], ACT.Ln, bias=1.0).then_inc(ls_act, 1)
                    c = slice(512 * n, 512 * n + 512)
                    act.wait_ge(gG_dve, n + 1)
                    act.activation(q_dec[:, :, c], g_l[:, :, :], ACT.Exp, scale=1.0 / 16).then_inc(ge_act, 1)
                    act.activation(k_inv[:, :, c], g_l[:, :, :], ACT.Exp, scale=-1.0 / 16).then_inc(ge_act, 1)
                    act.wait_ge(gD_dve, n + 1)
                    act.activation(k_end[:, :, c], g_u[:, :, :], ACT.Exp, scale=1.0 / 16).then_inc(ge_act, 1)
                elif kind == "qk":
                    s = w[0]
                    p, t = divmod(s, TT)
                    if s == 0:
                        act.wait_ge(prep_dve, 1)
                        act.wait_ge(g0_dve, 8)
                        act.wait_ge(tr_pe, at("tr", TT + 1, 1))
                    if s >= 2:
                        act.wait_ge(o_pe, at("o", s - 2))
                    copy(q_hi[:, s % 2, 0:4:3, :], q_dec[:, p, cols(t)].rearrange("p (j c) -> p j c", j=2))
                    copy(k_hi[:, s % 2, :], k_inv[:, p, cols(t)]).then_inc(qk_act, 1)
                elif kind == "kdT":
                    s = w[0]
                    act.wait_ge(kd_pe, s + 1)
                    if s >= 2:
                        act.wait_ge(kv_pe, at("kv", s - 2))
                    copy(ke_hi[:, s % 2, :], bank1[:, 0:P]).then_inc(kd_act, 1)
                elif kind == "proj" and w[0] < GLA_STEPS:
                    s = w[0]
                    act.wait_ge(pj_pe, s + 1)
                    if s >= 2:
                        act.wait_ge(o_pe, at("o", s - 2))
                    copy(v_hi[:, s % 2, :], bank0[:, 0:256])
                    if s:
                        act.wait_ge(pj_dve, s)
                    act.activation(tanh_g[:, :], bank0[:, 256:512], ACT.Tanh, scale=0.5).then_inc(pj_act, 1)
                elif kind == "sc":
                    s = w[0]
                    act.wait_ge(sc_cp, s + 1)
                    if s:
                        act.wait_ge(o_pe, at("o", s - 1))
                    copy(sc_hi[:, :, :], sc_f[:, :, :]).then_inc(sc_act, 1)
                elif kind == "kv":
                    s = w[0]
                    for n in new_states(s):
                        act.wait_ge(st_dve, state_no(s, n))
                        if s >= 2:
                            act.wait_ge(o_pe, at("o", s - 2))
                        copy(st_hi[:, n % 4, :], state[:, n % 2, :]).then_inc(st_act, 1)
                elif kind == "o":
                    s = w[0]
                    act.wait_ge(o_pe, at("o", s))
                    for hh in range(2):
                        square(banks[6 + hh][:, 0:P], sq_o[:, s % 2, hh:hh + 1], o_act, 2 * s + hh + 1)
                elif kind == "proj":
                    s = w[0]
                    i = s - GLA_STEPS
                    act.wait_ge(pj_pe, s + 1)
                    if i >= 2:
                        act.wait_ge(ring_pe, TR[("TQK", i - 2)] + 1)
                    copy(qk_tok[:, i % 2, :, ROPE:DQK],
                         bank0[:, 0:256].rearrange("p (j c) -> p j c", j=4)[:, :, ROPE:DQK])
                    wait(act, pv_pe, i - NV + TT)
                    copy(dv_hi[:, i % NV, :], bank0[:, 256:384])
                    act.wait_ge(pj_dve, s)
                    act.activation(tanh_g[:, 0:P], bank0[:, 384:512], ACT.Tanh, scale=0.5).then_inc(pj_act, 1)
                elif kind in ("TQK", "T", "MT", "HT", "PT"):
                    act.wait_ge(ring_pe, TR[stage] + 1)
                    if stage == ("TQK", 0):
                        act.wait_ge(qk_dve, GLA_STEPS)
                        act.wait_ge(kd_pe, GLA_STEPS)
                    elif kind == "TQK":
                        act.wait_ge(s_pe, w[0])
                    elif stage == ("T", 0, 0):
                        act.wait_ge(of_dve, GLA_STEPS)
                    elif kind == "T":
                        act.wait_ge(pv_pe, w[0])
                    elif kind == "MT":
                        act.wait_ge(pj_pe, GLA_STEPS + DIFF_STEPS)
                    elif kind == "HT":
                        act.wait_ge(pr_pe, PJ[("X", 1, w[0])] + 1 if w[0] < 4 else PJ[("Q", 0, 3, 1)] + 1)
                    elif w[1] or w[0]:
                        prev = ("O", w[0], w[1] - 1, 1) if w[1] else ("O", 0, XH - 1, 1)
                        act.wait_ge(pr_pe, PJ[prev] + 1)
                    hi, _, ps = ring_job(stage)
                    copy(hi, ps).then_inc(ring_act, 1)
                elif kind == "S":
                    i = w[0]
                    n = P * (i % TT + 1)
                    act.wait_ge(s_max, i + 1)
                    if i:
                        act.wait_ge(ring_pe, TR[("T", i - 1, (i - 1) % TT // 4)] + 1)
                    for m in range(2):
                        last = act.activation(
                            prob[:, m, 0:n], wide[:, 2 * m:2 * m + 2, :].rearrange("p j c -> p (j c)")[:, 0:n],
                            ACT.Exp, scale=DQK ** -0.5, bias=neg_maxs[:, i % 2, m:m + 1],
                            accum_out=exp_sum[:, i % 2, m:m + 1])
                    last.then_inc(s_act, 1)
                elif kind == "PV":
                    i = w[0]
                    act.wait_ge(pv_pe, i + 1)
                    square(bank1[:, 0:P], sq_o[:, i % 2, 0:1], pv_act, i + 1)
                elif kind in ("Ke", "V", "Q", "O"):
                    job = ("K", w[0]) if kind == "Ke" else stage
                    act.wait_ge(pr_pe, PJ[job] + 1)
                    if stage == ("Ke", 0):
                        act.wait_ge(pf_dve, DIFF_STEPS)
                    if stage == ("O", 0, 0, 0):
                        act.wait_ge(pr_pe, PJ[("X", 1, TT - 1)] + 1)
                    if stage == ("O", 1, 0, 0):
                        act.wait_ge(pr_pe, PJ[("C", 0, 1, 3)] + 1)
                    if kind == "Q" and w[0] + w[1]:
                        prev = ("SC", w[0], w[1] - 1) if w[1] else ("SC", 0, XH - 1)
                        act.wait_ge(x_pe, at(*prev))
                    hi, _, ps, scale = late_job(job)
                    copy(hi, ps, 1.0 if scale is None else scale).then_inc(pr_act, 1)
                elif kind == "nsq":
                    t = w[0]
                    g = ("X", 1, t)
                    act.wait_ge(pr_dve, PJ[g] + 1)
                    square(x_res[:, t, :], sq_x[:, t:t + 1], n_act, at("nsq", t))
                elif kind == "soft":
                    u = at("soft", *w)
                    act.wait_ge(x_max, u)
                    if u > 1:
                        act.wait_ge(ring_pe, TR[("PT", *divmod(u - 2, XH), 1)] + 1)
                    else:
                        act.wait_ge(ring_pe, TR[("MT", TT - 2, 1)] + 1)
                    for j in range(4):
                        t = 4 * w[0] + j
                        last = act.activation(
                            tile_a[:, M * j:M * j + M], wide[:, 2 + j // 2, M * (j % 2):M * (j % 2) + M],
                            ACT.Exp, scale=rs_x[:, t:t + 1], bias=x_negmaxs[:, j:j + 1],
                            accum_out=x_sum[:, j:j + 1])
                    last.then_inc(x_act, 1)
                elif kind == "fin":
                    t = w[0]
                    act.wait_ge(pr_dve, PJ[("C", t // 4, 1, t % 4)] + 1)
                    square(x_res[:, t, :], sq_x[:, TT + t:TT + t + 1], f_act, at("fin", t))

        @block.vector
        def _(dve):
            steps = [0]

            def then_wait(ins):
                steps[0] += 1
                ins.then_inc(dve_step, 1)
                dve.wait_ge(dve_step, steps[0])

            def lo_part(dst, src, hi, scale=None):
                if scale is None:
                    return dve.tensor_tensor(dst, src, hi.bitcast(F32), ALU.subtract)
                return dve.scalar_tensor_tensor(dst, src, scale, hi.bitcast(F32), ALU.mult, ALU.subtract)

            for stage in PLAN:
                kind, *w = stage
                if kind == "zeros":
                    dve.memset(ga_both[:, :, 2 * RANK:P].bitcast(F32), 0.0)
                    dve.memset(row_pick[:, :], 0.0)
                    dve.memset(row_neg[:, :], 0.0)
                    then_wait(dve.memset(g_keep[:, :], 1.0))
                    for r in (0, DQK):
                        dve.memset(row_pick[r:r + 1, 0:CH], 1.0)
                        dve.memset(row_neg[r:r + 1, :], NEG)
                    then_wait(dve.memset(g_keep[:, :].rearrange("p (j c) -> p j c", c=CH)[:, :, 0], 0.0))
                elif kind == "const":
                    dve.wait_ge(d_const, 16 * 13)
                    then_wait(dve.tensor_tensor(ga_raw[:, :, :], ga_raw[:, :, :],
                                                nw_mix[:, :].unsqueeze(2).to_broadcast([P, KT, RANK]), ALU.mult))
                    ga_hi, ga_lo = ga_both[:, :, 0:RANK], ga_both[:, :, RANK:2 * RANK]
                    then_wait(dve.tensor_copy(ga_hi, ga_raw[:, :, :]))
                    lo_part(ga_lo, ga_raw[:, :, :], ga_hi).then_inc(dve_c, 1)
                elif kind == "rope":
                    then_wait(dve.tensor_tensor(lam_pr[:, :, :], lam_in[:, 0:4:2, :], lam_in[:, 1:4:2, :], ALU.mult))
                    dve.tensor_reduce(lam_s[:, 0:2], lam_pr[:, :, :], AX.X, ALU.add).then_inc(dve_c, 1)
                    then_wait(dve.tensor_copy(pos_f[:, :], pos_i[:, :]))
                    inv = (THETA ** (-np.arange(0, ROPE, 2, dtype=np.float32) / ROPE)).astype(np.float32)
                    for j in range(ROPE // 2):
                        last = dve.tensor_scalar(ang[:, :, j], pos_f[:, :], float(inv[j]), None, ALU.mult)
                    then_wait(last)
                    then_wait(dve.tensor_scalar(ang_k[:, :, :], ang[:, :, :], 1.0 / (2 * math.pi), None, ALU.mult))
                    then_wait(dve.tensor_copy(ang_f[:, :, :], ang_k[:, :, :]))
                    turn1 = 6.28125
                    turn2 = round((2 * math.pi - turn1) * 2 ** 17) / 2 ** 17
                    turn3 = 2 * math.pi - turn1 - turn2
                    for part in (turn1, turn2, turn3):
                        then_wait(dve.scalar_tensor_tensor(ang[:, :, :], ang_f[:, :, :], -part, ang[:, :, :],
                                                           ALU.mult, ALU.add))
                    dve.tensor_scalar(ang2[:, 0, :, :], ang[:, :, :], math.pi / 2, None, ALU.add)
                    then_wait(dve.tensor_copy(ang2[:, 1, :, :], ang[:, :, :]))
                    for op, by in ((ALU.is_gt, math.pi), (ALU.is_lt, -math.pi)):
                        then_wait(dve.tensor_scalar(ang_w[:, :, :, :], ang2[:, :, :, :], by, None, op))
                        then_wait(dve.scalar_tensor_tensor(ang2[:, :, :, :], ang_w[:, :, :, :], -2 * by,
                                                           ang2[:, :, :, :], ALU.mult, ALU.add))
                    dve.tensor_scalar(ang2[:, :, :, :], ang2[:, :, :, :], 3.1415925, -3.1415925,
                                      ALU.min, ALU.max).then_inc(dve_c, 1)
                    dve.wait_ge(act_c, 1)
                    h = ROPE // 2
                    dve.tensor_copy(rope_c[:, :, 0:h], sin2[:, 0, :, :])
                    dve.tensor_copy(rope_c[:, :, h:ROPE], sin2[:, 0, :, :])
                    dve.tensor_scalar(rope_s[:, :, 0:h], sin2[:, 1, :, :], -1.0, None, ALU.mult)
                    dve.tensor_copy(rope_s[:, :, h:ROPE], sin2[:, 1, :, :]).then_inc(dve_c, 1)
                    dve.tensor_scalar(scale_out[:, 0:1], nw_head[:, 0:1], 0.5, None, ALU.mult)
                    dve.tensor_scalar(scale_out[:, 1:2], nw_head[:, 1:2], 0.5 * (1.0 - LAM_INIT), None,
                                      ALU.mult).then_inc(dve_c, 1)
                    dve.wait_ge(act_c, 2)
                    then_wait(dve.scalar_tensor_tensor(neg_lam[:, :], lam_s[:, 3:4], -LAM_INIT, lam_s[:, 2:3],
                                                       ALU.add, ALU.subtract))
                elif kind == "sq":
                    t = w[0]
                    dve.wait_ge(sq_sum, at("sq", t))
                    dve.tensor_scalar(var_in[:, t:t + 1], sq_in[:, t:t + 1], 1.0 / D, EPS,
                                      ALU.mult, ALU.add).then_inc(var_ok, 1)
                elif kind == "tr":
                    hi, lo = input_dest(*w)
                    dve.wait_ge(tr_act, at(*stage))
                    lo_part(lo, banks[w[1]].rearrange("p (j c) -> p j c", j=4), hi).then_inc(tr_dve, 1)
                elif kind == "w":
                    n = w[0]
                    dve.wait_ge(w_act, n + 1)
                    _, scale = weight_tile(n)
                    lo_part(w_lo[:, n % NW, :], w_raw[:, n % NRAW, :], w_hi[:, n % NW, :],
                            scale).then_inc(w_dve, 1)
                elif kind == "ga":
                    dve.wait_ge(ga_pe, at(*stage))
                    dve.tensor_copy(gaT[:, :], banks[3][0:2 * RANK, :]).then_inc(ga_dve, 1)
                elif kind == "gate":
                    n = w[0]
                    dve.wait_ge(ls_act, n + 1)
                    then_wait(dve.scalar_tensor_tensor(g_u[:, :, :], g_u[:, :, :], 0.0, g_l[:, :, :],
                                                       ALU.min, ALU.subtract))
                    for p in range(NPAIR):
                        last = dve.tensor_tensor_scan(g_l[:, p, :], g_keep[:, :], g_u[:, p, :], 0.0,
                                                      ALU.mult, ALU.add)
                    last.then_inc(gG_dve, 1)
                    dve.wait_ge(gG_dve, n + 1)
                    G = g_l[:, :, :].rearrange("p a (j c) -> p (a j) c", c=CH)
                    dve.tensor_tensor(g_u[:, :, :].rearrange("p a (j c) -> p (a j) c", c=CH),
                                      G[:, :, CH - 1:CH].to_broadcast([P, NCH, CH]), G,
                                      ALU.subtract).then_inc(gD_dve, 1)
                    dve.wait_ge(ge_act, 3 * n + 3)
                    dve.tensor_copy(decay[:, :, 8 * n:8 * n + 8],
                                    q_dec[:, :, 512 * n + CH - 1:512 * n + 512:CH]).then_inc(ge_dve, 1)
                elif kind == "G0e":
                    n, c = w
                    g0 = 4 * n + c
                    ps = banks[4 + g0 % 4]
                    t = slice(512 * n, 512 * n + 512)
                    dve.wait_ge(g0_pe, g0 + 1)
                    dve.wait_ge(ge_dve, n + 1)
                    if c < NPAIR:
                        dve.scalar_tensor_tensor(q_dec[:, c, t], ps, GDK ** -0.5, q_dec[:, c, t],
                                                 ALU.mult, ALU.mult).then_inc(g0_dve, 1)
                    else:
                        p = c - NPAIR
                        dve.tensor_tensor(k_inv[:, p, t], ps, k_inv[:, p, t], ALU.mult)
                        dve.tensor_tensor(k_end[:, p, t], ps, k_end[:, p, t], ALU.mult).then_inc(g0_dve, 1)
                elif kind == "glaprep":
                    dve.wait_ge(pool_c, 6)
                    dve.wait_ge(tr_pe, at("tr", TT + 1, 1))
                    dve.wait_ge(tr_act, at("tr", TT + 1, 1))
                    dve.wait_ge(z_pe, 2)
                    dve.wait_ge(ga_pe, 2)
                    for b in (q_hi, q_lo):
                        dve.memset(b[:, :, 1:3, :].bitcast(F32), 0.0)
                    dve.memset(sc_f[:, :, :], 0.0).then_inc(prep_dve, 1)
                    dve.wait_ge(prep_dve, 1)
                elif kind == "qk":
                    s = w[0]
                    p, t = divmod(s, TT)
                    dve.wait_ge(qk_act, s + 1)
                    lo_part(q_lo[:, s % 2, 0:4:3, :], q_dec[:, p, cols(t)].rearrange("p (j c) -> p j c", j=2),
                            q_hi[:, s % 2, 0:4:3, :])
                    lo_part(k_lo[:, s % 2, :], k_inv[:, p, cols(t)], k_hi[:, s % 2, :]).then_inc(qk_dve, 1)
                elif kind == "kdT":
                    s = w[0]
                    dve.wait_ge(kd_act, s + 1)
                    lo_part(ke_lo[:, s % 2, :], bank1[:, 0:P], ke_hi[:, s % 2, :]).then_inc(kd_dve, 1)
                elif kind == "proj" and w[0] < GLA_STEPS:
                    s = w[0]
                    dve.wait_ge(pj_act, s + 1)
                    lo_part(v_lo[:, s % 2, :], bank0[:, 0:256], v_hi[:, s % 2, :])
                    wait(dve, of_dve, s - 1)
                    dve.scalar_tensor_tensor(gate[:, 256 * (s % 2):256 * (s % 2) + 256], tanh_g[:, :], 1.0,
                                             bank0[:, 256:512], ALU.add, ALU.mult).then_inc(pj_dve, 1)
                elif kind == "sc":
                    s = w[0]
                    dve.wait_ge(sc_pe, s + 1)
                    for hh in range(2):
                        last = dve.copy_predicated(sc_f[:, hh, :], gla_mask[:, :].bitcast(U32),
                                                   banks[2 + hh][:, 0:P])
                    last.then_inc(sc_cp, 1)
                    dve.wait_ge(sc_act, s + 1)
                    lo_part(sc_lo[:, :, :], sc_f[:, :, :], sc_hi[:, :, :]).then_inc(sc_dve, 1)
                elif kind == "kv":
                    s = w[0]
                    p, t = divmod(s, TT)
                    dve.wait_ge(kv_pe, s + 1)
                    for n in new_states(s):
                        kv = banks[4 + (n - 1) % 2][:, 0:256]
                        no = state_no(s, n)
                        wait(dve, st_dve, no - 1 if n > 1 else 0)
                        if n == 1:
                            dve.tensor_copy(state[:, 1, :], kv).then_inc(st_dve, 1)
                        else:
                            dve.scalar_tensor_tensor(state[:, n % 2, :], state[:, (n - 1) % 2, :],
                                                     decay[:, p, n - 1:n], kv,
                                                     ALU.mult, ALU.add).then_inc(st_dve, 1)
                    for n in new_states(s):
                        dve.wait_ge(st_act, state_no(s, n))
                        lo_part(st_lo[:, n % 4, :], state[:, n % 2, :], st_hi[:, n % 4, :]).then_inc(stl_dve, 1)
                elif kind == "o":
                    s = w[0]
                    dve.wait_ge(o_act, 2 * s + 2)
                    dve.tensor_scalar(var_o[:, s % 2, :], sq_o[:, s % 2, :], 1.0 / GDV, EPS,
                                      ALU.mult, ALU.add).then_inc(o_dve, 1)
                elif kind == "ofin":
                    s = w[0]
                    j = s % 2
                    dve.wait_ge(o_pool, s + 1)
                    if s >= 2:
                        dve.wait_ge(d_mixg[j], 16 * (s // 2))
                    for hh in range(2):
                        c = slice(256 * j + P * hh, 256 * j + P * hh + P)
                        last = dve.scalar_tensor_tensor(mix_out[:, c], banks[6 + hh][:, 0:P],
                                                        rs_o[:, j, hh:hh + 1], gate[:, c], ALU.mult, ALU.mult)
                    last.then_inc(of_dve, 1)
                elif kind == "proj":
                    s = w[0]
                    i = s - GLA_STEPS
                    t = i % TT
                    if i == 0:
                        dve.wait_ge(dve_c, 4)
                    dve.wait_ge(pj_act, s + 1)
                    lo_part(dv_lo[:, i % NV, :], bank0[:, 256:384], dv_hi[:, i % NV, :])
                    dve.wait_ge(of_dve, GLA_STEPS - (i < 2))
                    wait(dve, pf_dve, i - 3)
                    dve.scalar_tensor_tensor(gate[:, P * (i % 4):P * (i % 4) + P], tanh_g[:, 0:P], 1.0,
                                             bank0[:, 384:512], ALU.add, ALU.mult)
                    ps = bank0[:, 0:256].rearrange("p (j c) -> p j c", j=4)
                    rot = qk_tok[:, i % 2, :, 0:ROPE]
                    h = ROPE // 2
                    cs, sn = (x[:, t, :].unsqueeze(1).to_broadcast([P, 4, ROPE]) for x in (rope_c, rope_s))
                    if i >= 2:
                        dve.wait_ge(ring_pe, TR[("TQK", i - 2)] + 1)
                    dve.tensor_tensor(rot_s[:, :, 0:h], ps[:, :, h:ROPE], sn[:, :, 0:h], ALU.mult)
                    dve.tensor_tensor(rot_s[:, :, h:ROPE], ps[:, :, 0:h], sn[:, :, h:ROPE], ALU.mult)
                    then_wait(dve.tensor_tensor(rot_c[:, :, :], ps[:, :, 0:ROPE], cs, ALU.mult))
                    dve.tensor_tensor(rot, rot_c[:, :, :], rot_s[:, :, :], ALU.add).then_inc(pj_dve, 1)
                elif kind in ("TQK", "T", "MT", "HT", "PT"):
                    hi, lo, ps = ring_job(stage)
                    dve.wait_ge(ring_act, TR[stage] + 1)
                    lo_part(lo, ps, hi).then_inc(ring_dve, 1)
                elif kind == "S":
                    i = w[0]
                    n = P * (i % TT + 1)
                    dve.wait_ge(s_pe, i + 1)
                    both = wide[:, :, :].rearrange("p (m j) c -> p m (j c)", m=2)[:, :, 0:n]
                    then_wait(dve.tensor_reduce(neg_max[:, i % 2, :], both, AX.X, ALU.max, negate=True))
                    dve.tensor_scalar(neg_maxs[:, i % 2, :], neg_max[:, i % 2, :], DQK ** -0.5, None,
                                      ALU.mult).then_inc(s_max, 1)
                elif kind == "comb":
                    i = w[0]
                    j = i % 2
                    n = P * (i % TT + 1)
                    dve.wait_ge(s_act, i + 1)
                    then_wait(dve.reciprocal(inv_sum[:, :], exp_sum[:, j, 1:2]))
                    dve.scalar_tensor_tensor(eps_sum[:, j:j + 1], exp_sum[:, j, 0:1], EPS, exp_sum[:, j, 0:1],
                                             ALU.mult, ALU.mult)
                    then_wait(dve.scalar_tensor_tensor(map_ratio[:, :], inv_sum[:, :], exp_sum[:, j, 0:1],
                                                       neg_lam[:, :], ALU.mult, ALU.mult))
                    dve.scalar_tensor_tensor(prob[:, 0, 0:n], prob[:, 1, 0:n], map_ratio[:, :],
                                             prob[:, 0, 0:n], ALU.mult, ALU.add).then_inc(s_dve, 1)
                elif kind == "PV":
                    i = w[0]
                    j = i % 2
                    dve.wait_ge(pv_act, i + 1)
                    dve.scalar_tensor_tensor(var_o[:, j, 0:1], sq_o[:, j, 0:1], 1.0 / DV, eps_sum[:, j:j + 1],
                                             ALU.mult, ALU.add).then_inc(pv_dve, 1)
                elif kind == "pvfin":
                    i = w[0]
                    dve.wait_ge(pv_pool, i + 1)
                    if i < 4:
                        dve.wait_ge(d_mixg[i // 2], 16 * GLA_STEPS // 2)
                    else:
                        dve.wait_ge(d_mixd[i % 4], 16 * (i // 4))
                    c = slice(P * (i % 4), P * (i % 4) + P)
                    dve.scalar_tensor_tensor(mix_out[:, c], bank1[:, 0:P], rs_o[:, i % 2, 0:1], gate[:, c],
                                             ALU.mult, ALU.mult).then_inc(pf_dve, 1)
                elif kind in ("Ke", "V", "Q", "O"):
                    job = ("K", w[0]) if kind == "Ke" else stage
                    hi, lo, ps, scale = late_job(job)
                    dve.wait_ge(pr_act, SPLIT[stage] + 1)
                    lo_part(lo, ps, hi, scale).then_inc(pr_dve, 1)
                elif kind in ("X", "C"):
                    g, t = w[-2], w[-1] + (4 * w[0] if kind == "C" else 0)
                    dve.wait_ge(pr_pe, PJ[stage] + 1)
                    if kind == "X" and g == 0:
                        dve.wait_ge(d_xres[t], 16)
                    ps = banks[PJ_BANKS[PJ[stage] % 4]]
                    c = slice(WC * g, WC * g + WC)
                    dve.tensor_tensor(x_res[:, t, c], ps, x_res[:, t, c], ALU.add).then_inc(pr_dve, 1)
                elif kind == "nsq":
                    t = w[0]
                    dve.wait_ge(n_act, at("nsq", t))
                    dve.tensor_scalar(var_x[:, t:t + 1], sq_x[:, t:t + 1], 1.0 / D, EPS,
                                      ALU.mult, ALU.add).then_inc(n_dve, 1)
                elif kind == "SC":
                    dve.wait_ge(x_pe, at(*stage))
                    four = wide[:, 2:4, :].rearrange("p j (i c) -> p (j i) c", c=M)
                    then_wait(dve.tensor_reduce(x_negmax[:, :], four, AX.X, ALU.max, negate=True))
                    rs = rs_x[:, 4 * w[0]:4 * w[0] + 4]
                    dve.wait_ge(n_pool, at("nsq", 4 * w[0] + 3))
                    dve.tensor_tensor(x_negmaxs[:, :], x_negmax[:, :], rs, ALU.mult).then_inc(x_max, 1)
                elif kind == "soft":
                    dve.wait_ge(x_act, at(*stage))
                    then_wait(dve.reciprocal(x_inv[:, :], x_sum[:, :]))
                    pr = tile_a[:, :].rearrange("p (j c) -> p j c", c=M)
                    dve.tensor_tensor(pr, pr, x_inv[:, :].unsqueeze(2).to_broadcast([P, 4, M]),
                                      ALU.mult).then_inc(x_dve, 1)
                elif kind == "fin":
                    t = w[0]
                    c = slice(TT + t, TT + t + 1)
                    dve.wait_ge(f_act, at("fin", t))
                    dve.tensor_scalar(var_x[:, c], sq_x[:, c], 1.0 / D, EPS, ALU.mult, ALU.add).then_inc(f_dve, 1)
                    dve.wait_ge(d_fw, 16)
                    dve.wait_ge(f_pool, at("fin", t))
                    dve.scalar_tensor_tensor(x_res[:, t, :], x_res[:, t, :], rs_x[:, c], tile_b[:, :],
                                             ALU.mult, ALU.mult).then_inc(fo_dve, 1)

        @block.tensor
        def _(pe):
            def mm3(dst, l_hi, l_lo, r_hi, r_lo, start, stop):
                pe.matmul(dst, l_hi, r_hi, start=start, stop=False)
                pe.matmul(dst, l_hi, r_lo, start=False, stop=False)
                return pe.matmul(dst, l_lo, r_hi, start=False, stop=stop)

            def project(stage, dst, stationary, moving):
                g = GROUP_OF[stage]
                for k in range(KT):
                    n = g * KT + k
                    if stage in FIRST_USE:
                        pe.wait_ge(w_dve, n + 1)
                    slot = n % NW
                    l_hi, l_lo = stationary(k, slot)
                    r_hi, r_lo = moving(k, slot)
                    last = mm3(dst, l_hi, l_lo, r_hi, r_lo, k == 0, k == KT - 1)
                    if stage in LAST_USE:
                        last.then_inc(w_used, 1)
                return last

            def signal(ins, stage, sem_done):
                if stage in LAST_USE:
                    pe.wait_ge(w_used, (GROUP_OF[stage] + 1) * KT)
                    pe.nop().then_inc(sem_done, 1)
                else:
                    ins.then_inc(sem_done, 1)

            def weights(c, n=P):
                return lambda k, slot: (w_hi[:, slot, c:c + n], w_lo[:, slot, c:c + n])

            def activations(c):
                return lambda k, slot: (actT_hi[:, k, c], actT_lo[:, k, c])

            def memory_tokens(c):
                return lambda k, slot: (memT_hi[:, k, c], memT_lo[:, k, c])

            def late_bank(stage):
                wait(pe, pr_dve, PJ[stage] - 3)
                return banks[PJ_BANKS[PJ[stage] % 4]]

            def turn(stage, parts):
                wait(pe, ring_dve, TR[stage] - 1)
                ps = banks[6 + TR[stage] % 2]
                for j, src in enumerate(parts):
                    last = pe.transpose(ps[:, cols(j)], src, ident[:, :])
                last.then_inc(ring_pe, 1)

            for stage in PLAN:
                kind, *w = stage
                if kind == "sq" and w[0] == 0:
                    pe.wait_ge(pool_c, 4)
                elif kind == "tr":
                    t, kk = w
                    pe.wait_ge(scaled, at("scale", t))
                    wait(pe, tr_dve, at(*stage) - 2)
                    for j in range(4):
                        last = pe.transpose(banks[kk][:, cols(j)], stage_in[:, t % NSTAGE, cols(4 * kk + j)],
                                            ident[:, :])
                    last.then_inc(tr_pe, 1)
                elif kind == "ga":
                    n = w[0]
                    pe.wait_ge(dve_c, 1)
                    pe.wait_ge(tr_dve, at("tr", 4 * n + 3, 1))
                    wait(pe, z_act, n)
                    c = slice(512 * n, 512 * n + 512)
                    for k in range(KT):
                        pe.matmul(banks[3], ga_both[:, k, :], actT_hi[:, k, c], start=k == 0, stop=False)
                        last = pe.matmul(banks[3], ga_both[:, k, :], actT_lo[:, k, c], start=False, stop=k == KT - 1)
                    last.then_inc(ga_pe, 1)
                elif kind == "z":
                    n = w[0]
                    pe.wait_ge(ga_dve, n + 1)
                    for p in range(NPAIR):
                        last = pe.matmul(banks[2 + p], wa2[:, cols(p)], gaT[:, :], start=True, stop=True)
                    last.then_inc(z_pe, 1)
                elif kind == "G0":
                    n, c = w
                    g0 = 4 * n + c
                    pe.wait_ge(tr_dve, at("tr", 4 * n + 3, 1))
                    wait(pe, g0_dve, g0 - 3)
                    last = project(stage, banks[4 + g0 % 4], weights(P * c), activations(slice(512 * n, 512 * n + 512)))
                    signal(last, stage, g0_pe)
                elif kind == "kdT":
                    s = w[0]
                    p, t = divmod(s, TT)
                    if s == 0:
                        pe.wait_ge(g0_dve, 8)
                    wait(pe, kd_dve, s)
                    pe.transpose(bank1[:, 0:P], k_end[:, p, cols(t)], ident[:, :]).then_inc(kd_pe, 1)
                elif kind == "proj":
                    s = w[0]
                    wait(pe, pj_dve, s)
                    if s == 0:
                        pe.wait_ge(tr_dve, at("tr", TT + 1, 1))
                    last = project(stage, bank0[:, :], activations(cols(s % TT)),
                                   lambda k, slot: (w_hi[:, slot, :], w_lo[:, slot, :]))
                    signal(last, stage, pj_pe)
                elif kind == "sc":
                    s = w[0]
                    pe.wait_ge(qk_dve, s + 1)
                    wait(pe, sc_cp, s)
                    if s == 0:
                        pe.wait_ge(z_act, 2)
                    j = s % 2
                    parts = ((k_hi, q_hi), (k_hi, q_lo), (k_lo, q_hi))
                    for m, (l, r) in enumerate(parts):
                        for hh in range(2):
                            rows = slice(GDK * hh, GDK * hh + GDK)
                            last = pe.matmul(banks[2 + hh][:, 0:P], l[rows, j, :], r[rows, j, 0:4:3, :],
                                             start=m == 0, stop=m == 2)
                    last.then_inc(sc_pe, 1)
                elif kind == "kv":
                    s = w[0]
                    j = s % 2
                    pe.wait_ge(kd_dve, s + 1)
                    pe.wait_ge(pj_dve, s + 1)
                    wait(pe, st_dve, state_no(s - 1, new_states(s - 1)[-1]) if s else 0)
                    if s == 0:
                        pe.wait_ge(g0_dve, 8)
                    parts = ((ke_hi, v_hi), (ke_hi, v_lo), (ke_lo, v_hi))
                    for m, (l, r) in enumerate(parts):
                        for c in range(len(new_states(s))):
                            rows = slice(CH * c, CH * c + CH)
                            last = pe.matmul(banks[4 + c][:, 0:256], l[rows, j, :], r[rows, j, :],
                                             start=m == 0, stop=m == 2)
                    last.then_inc(kv_pe, 1)
                elif kind == "o":
                    s = w[0]
                    t = s % TT
                    j = s % 2
                    pe.wait_ge(sc_dve, s + 1)
                    pe.wait_ge(stl_dve, state_no(s, 2 * t + 1))
                    wait(pe, of_dve, s)
                    if s == 0:
                        pe.wait_ge(g0_dve, 8)
                    for hh in range(2):
                        o = banks[6 + hh][:, 0:P]
                        rows = slice(GDK * hh, GDK * hh + GDK)
                        e = cols(hh)
                        mm3(o, sc_hi[:, hh, :], sc_lo[:, hh, :], v_hi[:, j, e], v_lo[:, j, e], True, False)
                        for c in range(2):
                            n = 2 * t + c
                            if n:
                                q2 = slice(2 * c, 2 * c + 2)
                                last = mm3(o, q_hi[rows, j, q2, :].rearrange("p a c -> p (a c)"),
                                           q_lo[rows, j, q2, :].rearrange("p a c -> p (a c)"),
                                           st_hi[rows, n % 4, e], st_lo[rows, n % 4, e], False, c == 1)
                    last.then_inc(o_pe, 1)
                elif kind == "TQK":
                    i = w[0]
                    pe.wait_ge(pj_dve, GLA_STEPS + i + 1)
                    if i == 0:
                        pe.wait_ge(of_dve, GLA_STEPS)
                    tok = qk_tok[:, i % 2, :, :].rearrange("p (j m) c -> p j (m c)", j=2)
                    turn(stage, [tok[:, 0, :], tok[:, 1, :]])
                elif kind == "S":
                    i = w[0]
                    t = i % TT
                    n = P * (t + 1)
                    pe.wait_ge(ring_dve, TR[("TQK", i)] + 1)
                    wait(pe, s_act, i)
                    if i == 0:
                        pe.wait_ge(dve_c, 1)
                        pe.wait_ge(st_dve, state_no(GLA_STEPS - 1, NCH - 1))
                    for g in range(0, n, 512):
                        keys = slice(g, min(g + 512, n))
                        parts = ((qkT_hi, qkT_hi), (qkT_hi, qkT_lo), (qkT_lo, qkT_hi))
                        for m, (l, r) in enumerate(parts):
                            for half in range(2):
                                rows = slice(DQK * half, DQK * half + DQK)
                                last = pe.matmul(wide[:, 2 * half + g // 512, 0:keys.stop - g],
                                                 l[rows, 0, cols(t)], r[rows, 1, keys],
                                                 start=m == 0, stop=m == 2)
                            if m == 0 and keys.stop == n:
                                for half in range(2):
                                    rows = slice(DQK * half, DQK * half + DQK)
                                    c = (n - CH) % 512
                                    pe.matmul(wide[:, 2 * half + g // 512, c:c + CH], row_pick[rows, :],
                                              row_neg[rows, :], start=False, stop=False)
                    last.then_inc(s_pe, 1)
                elif kind == "T":
                    i, g = w
                    pe.wait_ge(s_dve, i + 1)
                    turn(stage, [prob[:, 0, cols(b)] for b in range(4 * g, min(4 * g + 4, i % TT + 1))])
                elif kind == "PV":
                    i = w[0]
                    t = i % TT
                    pe.wait_ge(ring_dve, TR[("T", i, t // 4)] + 1)
                    wait(pe, pf_dve, i)
                    if i == 0:
                        pe.wait_ge(kd_dve, GLA_STEPS)
                    for b in range(t + 1):
                        v = (i - t + b) % NV
                        last = mm3(bank1[:, 0:P], prT_hi[:, b, :], prT_lo[:, b, :],
                                   dv_hi[:, v, :], dv_lo[:, v, :], b == 0, b == t)
                    last.then_inc(pv_pe, 1)
                elif kind == "K":
                    ps = late_bank(stage)
                    if w[0] == 0:
                        pe.wait_ge(pj_dve, GLA_STEPS + DIFF_STEPS)
                    if w[0] == 1:
                        pe.wait_ge(s_act, DIFF_STEPS)
                    if w[0] == 3:
                        pe.wait_ge(pf_dve, DIFF_STEPS)
                    last = project(stage, ps[:, 0:M], weights(P * (w[0] % 4)), memory_tokens(slice(0, M)))
                    signal(last, stage, pr_pe)
                elif kind == "V":
                    last = project(stage, late_bank(stage), memory_tokens(cols(w[1])),
                                   lambda k, slot: (w_hi[:, slot, :], w_lo[:, slot, :]))
                    signal(last, stage, pr_pe)
                elif kind == "MT":
                    t, kk = w
                    pe.wait_ge(d_tile[t % 2], 16 * (t // 2 + 1))
                    turn(stage, [(tile_a, tile_b)[t % 2][:, cols(4 * kk + j)] for j in range(4)])
                elif kind == "X":
                    g, t = w
                    if g == 0:
                        pe.wait_ge(ring_dve, TR[("MT", t, 1)] + 1)
                    last = project(stage, late_bank(stage), activations(cols(t)),
                                   lambda k, slot: (w_hi[:, slot, :], w_lo[:, slot, :]))
                    signal(last, stage, pr_pe)
                elif kind == "HT":
                    t, kk = w
                    pe.wait_ge(pr_dve, PJ[("X", 1, t)] + 1)
                    turn(stage, [x_res[:, t, cols(4 * kk + j)] for j in range(4)])
                elif kind == "Q":
                    half, h, d = w
                    pe.wait_ge(ring_dve, TR[("HT", 4 * half + 3, 1)] + 1)
                    last = project(stage, late_bank(stage), weights(P * (2 * (h % 2) + d)),
                                   activations(slice(0, 512)))
                    signal(last, stage, pr_pe)
                elif kind == "SC":
                    half, h = w
                    pe.wait_ge(pr_dve, PJ[("Q", half, h, 1)] + 1)
                    wait(pe, x_act, at(*stage) - 1)
                    for t in range(4):
                        for d in range(2):
                            last = mm3(wide[:, 2 + t // 2, M * (t % 2):M * (t % 2) + M],
                                       cq_hi[:, d, cols(t)], cq_lo[:, d, cols(t)],
                                       ck_hi[:, 2 * h + d, :], ck_lo[:, 2 * h + d, :], d == 0, d == 1)
                    last.then_inc(x_pe, 1)
                elif kind == "PT":
                    half, h, m = w
                    pe.wait_ge(x_dve, at("soft", half, h))
                    turn(stage, [tile_a[:, M * t + P * m:M * t + P * m + P] for t in range(4)])
                elif kind == "O":
                    half, h, d = w
                    pe.wait_ge(ring_dve, TR[("PT", half, h, 1)] + 1)
                    ps = late_bank(stage)
                    c = slice(XD * h + P * d, XD * h + P * d + P)
                    for m in range(MT):
                        last = mm3(ps, cv_hi[:, m, c], cv_lo[:, m, c], cpT_hi[:, m, :], cpT_lo[:, m, :],
                                   m == 0, m == MT - 1)
                    last.then_inc(pr_pe, 1)
                elif kind == "C":
                    half, g, t = w
                    pe.wait_ge(pr_dve, PJ[("O", half, XH - 2, 1)] + 1)

                    def outputs(k, slot):
                        if k == KT - 2:
                            pe.wait_ge(pr_dve, PJ[("O", half, XH - 1, 1)] + 1)
                        return actT_hi[:, k, 512 + P * t:640 + P * t], actT_lo[:, k, 512 + P * t:640 + P * t]

                    last = project(stage, late_bank(stage), outputs,
                                   lambda k, slot: (w_hi[:, slot, :], w_lo[:, slot, :]))
                    signal(last, stage, pr_pe)


NAMES = ["x", "mem", "positions", "norm_mix_w", "w_in", "w_alpha2", "b_alpha2", "gla_norm_w", "lam_q1", "lam_k1",
         "lam_q2", "lam_k2", "diff_norm_w", "w_out", "norm_cross_w", "norm_mem_w", "w_cq", "w_ckv", "w_co",
         "final_norm_w"]


def kernel(**inputs):
    import concourse.bacc as bacc
    from concourse.bass_utils import run_bass_kernel_spmd as run

    nc = bacc.Bacc("TRN2", target_bir_lowering=False, num_devices=1, dynamic_dma_scratch_size=4096)
    arrays, args = {}, {}
    for name in NAMES:
        array = np.ascontiguousarray(inputs[name])
        arrays[f"in_{name}"] = array
        args[name] = nc.dram_tensor(f"in_{name}", array.shape, mybir.dt.from_np(array.dtype),
                                    kind="ExternalInput").ap()
    out = nc.dram_tensor("out", (1, S, D), F32, kind="ExternalOutput").ap()
    with nc.allow_non_contiguous_dma(reason="norm weights and positions, a few KB, onto partitions"):
        build(nc, args, out)
    return run(nc, [arrays], core_ids=[0]).results[0]["out"]
```
